# Optimizing a Trainium2 kernel written in Bass

```python
import math
import jax, jax.numpy as jnp
from jax import lax
import numpy as np

D_MODEL = 2048
BATCH = 1
SEQ = 256
DEPTH = 2

RET_HEADS = 4
RET_HEAD_DIM = D_MODEL // 8
RET_V_DIM = D_MODEL // 8
RET_W = RET_HEADS * RET_HEAD_DIM
RET_VW = RET_HEADS * RET_V_DIM
RET_CHUNK = 128
ROPE_BASE = 10000.0
LRU_W = D_MODEL // 2
LRU_BLOCKS = 8
LRU_BW = LRU_W // LRU_BLOCKS
LRU_CONV = 4
LRU_C = 8.0
MOBA_HEADS = 16
MOBA_HEAD_DIM = D_MODEL // MOBA_HEADS
MOBA_W = MOBA_HEADS * MOBA_HEAD_DIM
MOBA_BLOCK = 256
MOBA_TOPK = 3
MOBA_QCHUNK = 32
REL_BUCKETS = 32
REL_MAX_DIST = 128
D_FF = 11 * D_MODEL // 4
FFN_CONV = 3
EPS = 1e-6

EV_IN = 3 * RET_W + RET_VW + 2 * LRU_W
EV_CAT = RET_VW + LRU_W
OD_IN = 3 * MOBA_W

kernel_name = "hybrid_retention_rglru_moba_convffn"

def rmsnorm(x, g):
    x32 = x.astype(jnp.float32)
    y = x32 * lax.rsqrt(jnp.mean(x32 * x32, axis=-1, keepdims=True) + EPS)
    return (y * g.astype(jnp.float32)).astype(x.dtype)

def causal_dwconv(x, w, b):
    width, c = w.shape
    y = lax.conv_general_dilated(x, w.astype(x.dtype)[:, None, :], window_strides=(1,),
                                 padding=[(width - 1, 0)],
                                 dimension_numbers=('NWC', 'WIO', 'NWC'),
                                 feature_group_count=c)
    return y + b.astype(x.dtype)

def rotary(x, pos):
    half = x.shape[-1] // 2
    freqs = ROPE_BASE ** (-jnp.arange(half, dtype=jnp.float32) / half)
    ang = pos.astype(jnp.float32)[:, None] * freqs[None, :]
    cos = jnp.cos(ang)[None, :, None, :]
    sin = jnp.sin(ang)[None, :, None, :]
    x32 = x.astype(jnp.float32)
    x1, x2 = x32[..., :half], x32[..., half:]
    return jnp.concatenate([x1 * cos - x2 * sin, x1 * sin + x2 * cos], axis=-1).astype(x.dtype)

def retention(q, k, v):
    b_, s_, h_, dk = q.shape
    dv = v.shape[-1]
    n = s_ // RET_CHUNK
    pos = jnp.arange(s_)
    q = rotary(q, pos)
    k = rotary(k, pos) * (dk ** -0.5)
    log_g = jnp.log1p(-jnp.exp2(-5.0 - jnp.arange(h_, dtype=jnp.float32)))
    i = jnp.arange(RET_CHUNK)
    diff = i[:, None] - i[None, :]
    decay = jnp.where(diff >= 0, jnp.exp(log_g[:, None, None] * jnp.maximum(diff, 0)), 0.0)
    zeta = jnp.exp(log_g[None, :] * (RET_CHUNK - 1 - i)[:, None])
    xi = jnp.exp(log_g[None, :] * (i + 1)[:, None])
    g_chunk = jnp.exp(log_g * RET_CHUNK)
    qc = q.reshape(b_, n, RET_CHUNK, h_, dk)
    kc = k.reshape(b_, n, RET_CHUNK, h_, dk)
    vc = v.reshape(b_, n, RET_CHUNK, h_, dv)
    scores = jnp.einsum('bnihd,bnjhd->bnhij', qc, kc) * decay
    inner = jnp.einsum('bnhij,bnjhe->bnihe', scores, vc)
    kv = jnp.einsum('bnjhd,bnjhe->nbhde', kc * zeta[:, :, None], vc)

    def step(state, kv_n):
        return g_chunk[None, :, None, None] * state + kv_n, state

    _, state_prev = lax.scan(step, jnp.zeros((b_, h_, dk, dv), kv.dtype), kv)
    cross = jnp.einsum('bnihd,nbhde->bnihe', qc, state_prev) * xi[:, :, None]
    return (inner + cross).reshape(b_, s_, h_, dv).astype(v.dtype)

def rglru_branch(xl, gl, conv_w, conv_b, w_a, b_a, w_i, b_i, lam):
    b_, s_, w_ = xl.shape
    xc = causal_dwconv(xl, conv_w, conv_b)
    xb = xc.reshape(b_, s_, LRU_BLOCKS, LRU_BW)
    r = jax.nn.sigmoid((jnp.einsum('bsgi,gij->bsgj', xb, w_a).reshape(b_, s_, w_) + b_a).astype(jnp.float32))
    gi = jax.nn.sigmoid((jnp.einsum('bsgi,gij->bsgj', xb, w_i).reshape(b_, s_, w_) + b_i).astype(jnp.float32))
    log_a = -LRU_C * r * jax.nn.softplus(-lam.astype(jnp.float32))
    a = jnp.exp(log_a)
    u = jnp.sqrt(-jnp.expm1(2.0 * log_a)) * (gi * xc.astype(jnp.float32))

    def combine(left, right):
        a1, b1 = left
        a2, b2 = right
        return a1 * a2, a2 * b1 + b2

    _, h = lax.associative_scan(combine, (a, u), axis=1)
    return h.astype(xl.dtype) * jax.nn.gelu(gl)

def even_mixer(h, w_in, ret_norm, conv_w, conv_b, w_a, b_a, w_i, b_i, lam, w_out):
    b_, s_, _ = h.shape
    proj = h @ w_in
    cuts = np.cumsum([RET_W, RET_W, RET_VW, RET_VW, LRU_W])
    q, k, v, g, xl, gl = jnp.split(proj, cuts, axis=-1)
    q = q.reshape(b_, s_, RET_HEADS, RET_HEAD_DIM)
    k = k.reshape(b_, s_, RET_HEADS, RET_HEAD_DIM)
    v = v.reshape(b_, s_, RET_HEADS, RET_V_DIM)
    ret = retention(q, k, v)
    ret = rmsnorm(ret, ret_norm.reshape(RET_HEADS, RET_V_DIM)).reshape(b_, s_, RET_VW)
    ret = ret * jax.nn.silu(g)
    lru = rglru_branch(xl, gl, conv_w, conv_b, w_a, b_a, w_i, b_i, lam)
    return jnp.concatenate([ret, lru], axis=-1) @ w_out

def t5_bucket(dist):
    n = jnp.maximum(dist, 0)
    max_exact = REL_BUCKETS // 2
    nf = jnp.maximum(n, 1).astype(jnp.float32)
    large = max_exact + (jnp.log(nf / max_exact) / math.log(REL_MAX_DIST / max_exact)
                         * (REL_BUCKETS - max_exact)).astype(jnp.int32)
    large = jnp.minimum(large, REL_BUCKETS - 1)
    return jnp.where(n < max_exact, n, large)

def moba_attention(q, k, v, rel_bias):
    b_, s_, h_, d_ = q.shape
    nb = -(-s_ // MOBA_BLOCK)
    pad = nb * MOBA_BLOCK - s_
    kp = jnp.pad(k, ((0, 0), (0, pad), (0, 0), (0, 0)))
    vp = jnp.pad(v, ((0, 0), (0, pad), (0, 0), (0, 0)))
    kb = kp.reshape(b_, nb, MOBA_BLOCK, h_, d_).transpose(0, 3, 1, 2, 4)
    vb = vp.reshape(b_, nb, MOBA_BLOCK, h_, d_).transpose(0, 3, 1, 2, 4)
    kmean = jnp.mean(kb.astype(jnp.float32), axis=3)
    qh = q.transpose(0, 2, 1, 3)
    gate = jnp.einsum('bhsd,bhnd->bhsn', qh.astype(jnp.float32), kmean)
    own = jnp.arange(s_) // MOBA_BLOCK
    fully_past = jnp.arange(nb)[None, :] < own[:, None]
    gate = jnp.where(fully_past, gate, -jnp.inf)
    k_eff = min(MOBA_TOPK, nb)
    _, sel = lax.top_k(gate, k_eff)
    sel = sel.astype(jnp.int32)
    nc = s_ // MOBA_QCHUNK
    q_chunks = qh.reshape(b_, h_, nc, MOBA_QCHUNK, d_).transpose(0, 2, 1, 3, 4)
    sel_chunks = sel.reshape(b_, h_, nc, MOBA_QCHUNK, k_eff).transpose(0, 2, 1, 3, 4)
    starts = jnp.arange(nc, dtype=jnp.int32) * MOBA_QCHUNK
    rel_t = rel_bias.T.astype(jnp.float32)
    gather = jax.vmap(lambda blocks, idx: blocks[idx])

    def per_batch(bargs):
        q_b, sel_b, kb_b, vb_b = bargs

        def per_chunk(cargs):
            q_c, sel_c, c0 = cargs
            k_sel = gather(kb_b, sel_c)
            v_sel = gather(vb_b, sel_c)
            qpos = c0 + jnp.arange(MOBA_QCHUNK)
            kpos_sel = sel_c[..., None] * MOBA_BLOCK + jnp.arange(MOBA_BLOCK)
            bucket_sel = t5_bucket(qpos[None, :, None, None] - kpos_sel)
            bias_sel = jnp.take_along_axis(rel_t, bucket_sel.reshape(h_, -1), axis=1).reshape(kpos_sel.shape)
            valid = (jnp.arange(k_eff)[None, :] < (qpos // MOBA_BLOCK)[:, None])[None, :, :, None]
            l_sel = jnp.einsum('hqd,hqkjd->hqkj', q_c, k_sel).astype(jnp.float32) + bias_sel
            l_sel = jnp.where(valid, l_sel, -jnp.inf).reshape(h_, MOBA_QCHUNK, k_eff * MOBA_BLOCK)
            blk = c0 // MOBA_BLOCK
            k_own = lax.dynamic_index_in_dim(kb_b, blk, axis=1, keepdims=False)
            v_own = lax.dynamic_index_in_dim(vb_b, blk, axis=1, keepdims=False)
            kpos_own = blk * MOBA_BLOCK + jnp.arange(MOBA_BLOCK)
            dist_own = qpos[:, None] - kpos_own[None, :]
            l_own = jnp.einsum('hqd,hjd->hqj', q_c, k_own).astype(jnp.float32) + rel_t[:, t5_bucket(dist_own)]
            l_own = jnp.where((dist_own >= 0)[None], l_own, -jnp.inf)
            p = jax.nn.softmax(jnp.concatenate([l_sel, l_own], axis=-1), axis=-1)
            p_sel = p[..., :k_eff * MOBA_BLOCK].astype(v_sel.dtype)
            p_own = p[..., k_eff * MOBA_BLOCK:].astype(v_own.dtype)
            out = jnp.einsum('hqj,hqjd->hqd', p_sel, v_sel.reshape(h_, MOBA_QCHUNK, k_eff * MOBA_BLOCK, d_))
            return out + jnp.einsum('hqj,hjd->hqd', p_own, v_own)

        return lax.map(per_chunk, (q_b, sel_b, starts))

    out = lax.map(per_batch, (q_chunks, sel_chunks, kb, vb))
    return out.transpose(0, 1, 3, 2, 4).reshape(b_, s_, h_, d_)

def odd_mixer(h, w_in, q_norm, k_norm, rel_bias, w_out):
    b_, s_, _ = h.shape
    q, k, v = jnp.split(h @ w_in, 3, axis=-1)
    q = rmsnorm(q.reshape(b_, s_, MOBA_HEADS, MOBA_HEAD_DIM), q_norm) * (MOBA_HEAD_DIM ** -0.5)
    k = rmsnorm(k.reshape(b_, s_, MOBA_HEADS, MOBA_HEAD_DIM), k_norm)
    v = v.reshape(b_, s_, MOBA_HEADS, MOBA_HEAD_DIM)
    o = moba_attention(q, k, v, rel_bias)
    return o.reshape(b_, s_, MOBA_W) @ w_out

def conv_ffn(h, w_up, conv_w, conv_b, w_down):
    u = causal_dwconv(h @ w_up, conv_w, conv_b)
    gate, val = jnp.split(u, 2, axis=-1)
    return (jax.nn.gelu(gate) * val) @ w_down

def setup_inputs(seed: int = 0) -> dict:
    key = jax.random.key(seed)
    ks = jax.random.split(key, 24)
    ne = (DEPTH + 1) // 2
    no = DEPTH // 2
    f32 = jnp.float32

    def nrm(k, shape, fan):
        return jax.random.normal(k, shape, f32) * (fan ** -0.5)

    def gain(k, shape):
        return 1.0 + 0.02 * jax.random.normal(k, shape, f32)

    def small(k, shape):
        return 0.01 * jax.random.normal(k, shape, f32)

    u = jax.random.uniform(ks[11], (ne, LRU_W), f32, minval=0.9, maxval=0.999)
    p = u ** (1.0 / LRU_C)
    lam = jnp.log(p) - jnp.log1p(-p)
    return {
        "x": jax.random.normal(ks[0], (BATCH, SEQ, D_MODEL), f32),
        "norm_mix": gain(ks[1], (DEPTH, D_MODEL)),
        "norm_ffn": gain(ks[2], (DEPTH, D_MODEL)),
        "ev_w_in": nrm(ks[3], (ne, D_MODEL, EV_IN), D_MODEL),
        "ret_norm": gain(ks[4], (ne, RET_VW)),
        "lru_conv_w": nrm(ks[5], (ne, LRU_CONV, LRU_W), LRU_CONV),
        "lru_conv_b": small(ks[6], (ne, LRU_W)),
        "lru_w_a": nrm(ks[7], (ne, LRU_BLOCKS, LRU_BW, LRU_BW), LRU_BW),
        "lru_b_a": small(ks[8], (ne, LRU_W)),
        "lru_w_i": nrm(ks[9], (ne, LRU_BLOCKS, LRU_BW, LRU_BW), LRU_BW),
        "lru_b_i": small(ks[10], (ne, LRU_W)),
        "lru_lambda": lam,
        "ev_w_out": nrm(ks[12], (ne, EV_CAT, D_MODEL), EV_CAT),
        "od_w_in": nrm(ks[13], (no, D_MODEL, OD_IN), D_MODEL),
        "q_norm": gain(ks[14], (no, MOBA_HEAD_DIM)),
        "k_norm": gain(ks[15], (no, MOBA_HEAD_DIM)),
        "od_w_out": nrm(ks[16], (no, MOBA_W, D_MODEL), MOBA_W),
        "rel_bias": 0.1 * jax.random.normal(ks[17], (REL_BUCKETS, MOBA_HEADS), f32),
        "ffn_w_up": nrm(ks[18], (DEPTH, D_MODEL, 2 * D_FF), D_MODEL),
        "ffn_conv_w": nrm(ks[19], (DEPTH, FFN_CONV, 2 * D_FF), FFN_CONV),
        "ffn_conv_b": small(ks[20], (DEPTH, 2 * D_FF)),
        "ffn_w_down": nrm(ks[21], (DEPTH, D_FF, D_MODEL), D_FF),
    }

def reference(x, norm_mix, norm_ffn, ev_w_in, ret_norm, lru_conv_w, lru_conv_b, lru_w_a, lru_b_a,
              lru_w_i, lru_b_i, lru_lambda, ev_w_out, od_w_in, q_norm, k_norm, od_w_out, rel_bias,
              ffn_w_up, ffn_conv_w, ffn_conv_b, ffn_w_down):
    for l in range(DEPTH):
        hn = rmsnorm(x, norm_mix[l])
        if l % 2 == 0:
            e = l // 2
            y = even_mixer(hn, ev_w_in[e], ret_norm[e], lru_conv_w[e], lru_conv_b[e], lru_w_a[e],
                           lru_b_a[e], lru_w_i[e], lru_b_i[e], lru_lambda[e], ev_w_out[e])
        else:
            o = l // 2
            y = odd_mixer(hn, od_w_in[o], q_norm[o], k_norm[o], rel_bias, od_w_out[o])
        x = x + y
        x = x + conv_ffn(rmsnorm(x, norm_ffn[l]), ffn_w_up[l], ffn_conv_w[l], ffn_conv_b[l], ffn_w_down[l])
    return x


_drawn_inputs = setup_inputs


def setup_inputs(seed=0):
    import zlib

    import numpy as np

    out = dict(_drawn_inputs(seed))
    spreads = {}
    factors = {'norm_ffn': 2.71,
     'ret_norm': 6.013,
     'lru_conv_b': 2.689,
     'lru_b_a': 64.0,
     'lru_b_i': 54.247,
     'q_norm': 8.0,
     'k_norm': 8.0,
     'rel_bias': 26.333,
     'ffn_conv_b': 5.542}
    for name, (base, spread) in spreads.items():
        noise = np.random.default_rng([zlib.crc32(name.encode()), seed]).standard_normal(out[name].shape)
        drawn = base * np.exp(spread * noise) if base else spread * noise
        out[name] = __import__('jax').numpy.asarray(drawn.astype(out[name].dtype))
    for name, factor in factors.items():
        out[name] = (out[name] * factor).astype(out[name].dtype)
    return out
```

```python
import numpy as np

import concourse.bass as bass
from concourse import mybir

F32, F32R = mybir.dt.float32, mybir.dt.float32r
ALU, ACT, AX = mybir.AluOpType, mybir.ActivationFunctionType, mybir.AxisListType

P = 128
D = 2048
S = 256
KT = D // P
D_FF = 11 * D // 4
FT = D_FF // P
NB = 512
BT = NB // P
CT = 2
RING = 4
KC = KT // CT
FC = FT // CT
PAIRS = D_FF // NB
OUTB = D // NB
EPS = 1e-6

RET_HEADS, RET_DIM = 4, 256
LRU_TAPS, FFN_TAPS = 4, 3
HEADS, HEAD_DIM = 16, 128
REL_BUCKETS, REL_MAX_DIST = 32, 128
MASKED = -1e30
LOG1P_TERMS = 10

PARAM_FIELDS = [("gain", 4 * KT), ("ret_norm", 8), ("lru_conv_w", LRU_TAPS * 8), ("lru_conv_b", 8),
                ("lru_b_a", 8), ("lru_b_i", 8), ("lru_lambda", 8), ("q_norm", 1), ("k_norm", 1),
                ("ffn_conv_w", 2 * FFN_TAPS * 2 * FT), ("ffn_conv_b", 2 * 2 * FT)]
PARAM_AT = {}
N_PARAMS = 0
for _name, _n in PARAM_FIELDS:
    PARAM_AT[_name] = N_PARAMS
    N_PARAMS += _n

EVEN_BLOCKS = [("xl", 0, 4096), ("xl", 1, 4608), ("gl", 0, 5120), ("gl", 1, 5632),
               ("q", 0, 0), ("k", 0, 1024), ("v", 0, 2048), ("g", 0, 3072),
               ("q", 1, 512), ("k", 1, 1536), ("v", 1, 2560), ("g", 1, 3584)]
ODD_BLOCKS = [(kind, i, at * D + i * NB) for i in range(4) for at, kind in enumerate("qkv")]
INB = len(EVEN_BLOCKS)
EVEN_GROUPS = [0, 1, 0, 1, 0, 0, 1, 0, 0, 1, 0, 0]
ODD_GROUPS = [0, 0, 1, 0, 0, 1, 0, 0, 1, 0, 0, 0]
LAYER_BLOCKS = INB + OUTB + 2 * PAIRS + OUTB
LAYER_TURNS = (INB * KC + OUTB * KC + 2 * PAIRS * KC + OUTB * FC) // RING


class Phase:

    def __init__(self, layer):
        self.layer = layer
        self.n_in = layer * LAYER_BLOCKS
        self.n_out = self.n_in + INB
        self.n_up = self.n_out + OUTB
        self.n_down = self.n_up + 2 * PAIRS
        self.q_in = layer * LAYER_TURNS
        self.q_out = self.q_in + INB * KC // RING
        self.q_up = self.q_out + OUTB * KC // RING
        self.q_down = self.q_up + 2 * PAIRS * KC // RING
        own_in = 10 if layer == 0 else 8
        self.cross_in = layer * (10 + OUTB + 2 * PAIRS + OUTB)
        self.cross_out = self.cross_in + own_in
        self.cross_up = self.cross_out + OUTB
        self.cross_down = self.cross_up + 2 * PAIRS
        self.normed_in = layer * (10 + 2 * PAIRS)
        self.normed_up = self.normed_in + own_in


class Steps:

    def __init__(self, eng, sem):
        self.eng, self.sem, self.base, self.n = eng, sem, 0, 0

    def __call__(self, instruction):
        self.n += 1
        instruction.then_inc(self.sem, 1)

    def sync(self):
        self.eng.wait_ge(self.sem, self.base + self.n)


def spread(ap, n):
    return bass.AP(ap.tensor, ap.offset, [ap.ap[0], [0, n], ap.ap[1]])


def build(nc, x_t, params, w_gates, rope, decay, rel_bias, buckets, identity,
          w_in0, w_out0, w_up0, w_down0, w_in1, w_out1, w_up1, w_down1, out_t):
    w_in, w_out = (w_in0, w_in1), (w_out0, w_out1)
    w_up, w_down = (w_up0, w_up1), (w_down0, w_down1)
    phases = (Phase(0), Phase(1))

    at = [(nc.sbuf_base + 31) // 32 * 32]

    def place(name, shape, dtype=F32, offset=None):
        size = int(np.prod(shape[1:])) * 4
        if offset is None:
            offset = at[0]
            at[0] += (size + 31) // 32 * 32
        return nc.alloc_sbuf_tensor_at(name, shape, dtype, offset=offset), offset

    raw, _ = place("raw", [P, RING, CT, NB])
    w_hi, _ = place("w_hi", [P, RING, CT, NB], F32R)
    w_lo, _ = place("w_lo", [P, RING, CT, NB], F32R)
    x_res, _ = place("x_res", [P, KT, S])
    xs, _ = place("xs", [P, KT, 2, S], F32R)
    act, act_at = place("act", [P, FT, 2, S], F32R)
    cross, _ = place("cross", [P, BT, S])
    h, _ = place("h", [P, BT, S])
    buf_g, _ = place("buf_g", [P, BT, S])
    buf_v, _ = place("buf_v", [P, BT, S])
    sumsq, _ = place("sumsq", [P, S])
    rstd, _ = place("rstd", [P, S + 2])
    par, _ = place("par", [P, N_PARAMS])
    ident, _ = place("ident", [P, P])
    ones, _ = place("ones", [P, P])
    lru_c, _ = place("lru_c", [P, 8])
    small, _ = place("small", [P, 4, 8])
    assert at[0] <= nc.sbuf_usable_end, (at[0], nc.sbuf_usable_end)
    hf = h[:, :, :].rearrange("p t s -> p (t s)")
    stat_y, stat_v, stat_sum = hf[:, 0:S + 2], hf[:, 260:260 + S + 2], h[:, 3, :]

    ws = [act_at + 16 * 2 * S * 4]

    def work(name, shape, offset=None):
        if offset is None:
            offset = ws[0]
            ws[0] += int(np.prod(shape[1:])) * 4
            assert ws[0] <= act_at + FT * 2 * S * 4, name
        return place(name, shape, F32, offset)

    xc, _ = work("xc", [P, 8, S])
    gl_gelu, _ = work("gl_gelu", [P, 8, S])
    lru_t, lru_t_at = work("lru_t", [P, BT, S])
    lru_w, _ = work("lru_w", [P, BT, S])
    rope_t, _ = work("rope_t", [P, 2, S])
    decay_t, _ = work("decay_t", [P, RET_HEADS, S])
    rq, _ = work("rq", [P, BT, S])
    rk, _ = work("rk", [P, BT, S])
    rv, rv_at = work("rv", [P, 2, NB])
    ret_gate, _ = work("ret_gate", [P, BT, S])
    rot_a, _ = work("rot_a", [P, BT, S])
    rot_b, _ = work("rot_b", [P, BT, S])
    gates_w, _ = work("gates_w", [P, 2, 8, P], rv_at)
    ret_s, _ = work("ret_s", [P, 2, 3 * P], lru_t_at)
    ret_o, ret_sq = rot_b, rot_a

    ws[0] = act_at + 16 * 2 * S * 4
    bias, _ = work("bias", [P, HEADS, S])
    aq, _ = work("aq", [P, 2, BT, S])
    ak, _ = work("ak", [P, 2, BT, S])
    av, _ = work("av", [P, 2, 2, NB])
    probs, _ = work("probs", [P, BT, 3 * P])
    probs_t, _ = work("probs_t", [P, BT, 3 * P])
    att_sq, _ = work("att_sq", [P, BT, S])
    rel_ext, _ = place("rel_ext", [P, HEADS], F32, act_at)
    bucket_t, _ = place("bucket_t", [P, 3 * P], F32, act_at + 64)
    line, _ = place("line", [P, 3 * P], F32, act_at + 64 + 3 * P * 4)
    bias_line = nc.dram_tensor("bias_line", (HEADS, 3 * P), F32, kind="Internal").ap()

    ps = nc.alloc_psum_tensor("ps", [P, 8, NB], F32)

    def sem(name):
        return nc.alloc_semaphore(name)

    landed = [sem(f"landed{s}") for s in range(RING)]
    hi_ready, lo_ready, chunk_used = sem("hi_ready"), sem("lo_ready"), sem("chunk_used")
    cross_copied, acc_drained, normed = sem("cross_copied"), sem("acc_drained"), sem("normed")
    x_loaded = [sem(f"x_loaded{j}") for j in range(4)]
    const_loaded, work_loaded = sem("const_loaded"), sem("work_loaded")
    consts_set = sem("consts_set")
    xs_hi, xs_lo, squared, ss_added, ss_ready = (
        sem("xs_hi"), sem("xs_lo"), sem("squared"), sem("ss_added"), sem("ss_ready"))
    stat_summed, stat_read, stat_rsq, rstd_ready = sem("stat_summed"), sem("stat_read"), sem("stat_rsq"), sem("rstd_ready")
    dve_step, act_step = sem("dve_step"), sem("act_step")
    tap_first, conv_done, gelu_done = sem("tap_first"), sem("conv_done"), sem("gelu_done")
    prod_ready, act_hi, act_lo = sem("prod_ready"), sem("act_hi"), sem("act_lo")
    lam_abs, lam_exp, lru_c_ready = sem("lam_abs"), sem("lam_exp"), sem("lru_c_ready")
    line_done, line_copied, line_stored = sem("line_done"), sem("line_copied"), sem("line_stored")
    bias_loaded = sem("bias_loaded")
    xc_first, xc_ready = sem("xc_first"), sem("xc_ready")
    gelu_gl = sem("gelu_gl")
    gates_done, gates_read, lru_tanh, lru_sqrt = sem("gates_done"), sem("gates_read"), sem("lru_tanh"), sem("lru_sqrt")
    mix_prod, mix_hi, mix_lo = sem("mix_prod"), sem("mix_hi"), sem("mix_lo")
    rot_ready, gate_silu = sem("rot_ready"), sem("gate_silu")
    ret_scored, ret_s_ready, ret_out = sem("ret_scored"), sem("ret_s_ready"), sem("ret_out")
    ret_squared, ret_copied, ret_summed, ret_rsq, ret_stat_read = (
        sem("ret_squared"), sem("ret_copied"), sem("ret_summed"), sem("ret_rsq"), sem("ret_stat_read"))
    qk_squared, qk_summed, qk_rsq, qk_stat_read, qk_ready = (
        sem("qk_squared"), sem("qk_summed"), sem("qk_rsq"), sem("qk_stat_read"), sem("qk_ready"))
    scored, negmax_ready, exp_done, probs_ready = (
        sem("scored"), sem("negmax_ready"), sem("exp_done"), sem("probs_ready"))
    turned, turned_copied, pv_done = sem("turned"), sem("turned_copied"), sem("pv_done")
    stored = sem("stored")

    def param(name, k=0):
        c = PARAM_AT[name] + k
        return par[:, c:c + 1]

    def tiles(bank, n=4):
        return ps[:, bank:bank + (n + 1) // 2, :].rearrange("p b (u s) -> p (b u) s", s=S)[:, 0:n, :]

    def chunk_end(q, c):
        return RING * q + c + 1

    MIX_ORDER = ([4, 5, 6, 7, 0, 1, 2, 3], list(range(KC)))

    block = nc.Block()
    block.__enter__()

    @block.sync
    def _(sp):
        def load(w, q, c, cols, rows):
            s = c % RING
            turn = q + c // RING
            if not (isinstance(turn, int) and turn == 0):
                sp.wait_ge(lo_ready, RING * (turn - 1) + s + 1)
            src = w[rows * CT * P:(rows + 1) * CT * P, cols].rearrange("(t p) n -> p t n", p=P)
            sp.dma_start(raw[:, s, :, :], src).then_inc(landed[s], 16)

        for ph in phases:
            l = ph.layer
            for b, (_, _, col) in enumerate(ODD_BLOCKS if l else EVEN_BLOCKS):
                for c in range(KC):
                    load(w_in[l], ph.q_in + 2 * b, c, slice(col, col + NB), c)
            for b in range(OUTB):
                for c in range(KC):
                    load(w_out[l], ph.q_out + 2 * b, c, slice(b * NB, (b + 1) * NB), MIX_ORDER[l][c])
            with sp.Fori(0, PAIRS) as j:
                for half in range(2):
                    for c in range(KC):
                        load(w_up[l], ph.q_up + 4 * j + 2 * half, c, bass.ds(j * NB + half * D_FF, NB), c)
            for b in range(OUTB):
                for c in range(FC):
                    load(w_down[l], ph.q_down, FC * b + c, slice(b * NB, (b + 1) * NB), c)

    @block.gpsimd
    def _(pool):
        nc.gpsimd.memset(ones[:, :], 1.0).then_inc(consts_set, 1)
        pool.wait_ge(consts_set, 1)
        nc.gpsimd.memset(rel_ext[REL_BUCKETS:REL_BUCKETS + 1, :], MASKED).then_inc(consts_set, 1)
        pool.wait_ge(line_copied, 1)
        pool.dma_start(bias_line[:, :], line[0:HEADS, :]).then_inc(line_stored, 16)
        pool.wait_ge(line_stored, 16)
        pool.wait_ge(chunk_used, RING * LAYER_TURNS)
        hankel = bass.AP(bias_line.tensor, 0, [[1, P], [3 * P, HEADS], [1, S]])
        pool.dma_start(bias[:, :, :], hankel).then_inc(bias_loaded, 16)
        for b in range(OUTB):
            pool.wait_ge(acc_drained, phases[1].n_down + b + 1)
            pool.dma_start(out_t[:, b * BT:(b + 1) * BT, :], x_res[:, b * BT:(b + 1) * BT, :]).then_inc(stored, 16)
        pool.wait_ge(stored, 16 * OUTB)

    @block.scalar
    def _(eng):
        act_f = nc.scalar.activation
        step = Steps(eng, act_step)
        for j in range(4):
            eng.dma_start(x_res[:, j * BT:(j + 1) * BT, :], x_t[:, j * BT:(j + 1) * BT, :]).then_inc(x_loaded[j], 16)
            if j == 0:
                eng.dma_start(par[:, :], params).then_inc(const_loaded, 16)
        eng.dma_start(rel_ext[0:REL_BUCKETS, :], rel_bias).then_inc(work_loaded, 16)
        eng.dma_start(bucket_t[0:REL_BUCKETS + 1, :], buckets).then_inc(work_loaded, 16)
        eng.dma_start(gates_w[:, :, :, :], w_gates).then_inc(work_loaded, 16)
        eng.dma_start(rope_t[:, :, :], rope).then_inc(work_loaded, 16)
        eng.dma_start(decay_t[:, :, :], decay).then_inc(work_loaded, 16)
        eng.dma_start(ident[:, :], identity).then_inc(work_loaded, 16)

        def split(q, c):
            s, turn = c % RING, q + c // RING
            eng.wait_ge(landed[s], 16 * (turn + 1))
            if not (isinstance(turn, int) and turn == 0):
                eng.wait_ge(chunk_used, RING * (turn - 1) + s + 1)
            act_f(w_hi[:, s, :, :], raw[:, s, :, :], ACT.Copy).then_inc(hi_ready, 1)

        def copy_cross(n, used, group):
            eng.wait_ge(chunk_used, used)
            if not (isinstance(n, int) and n == 0):
                eng.wait_ge(acc_drained, n)
            act_f(cross[:, :, :], ps[:, 4 * group:4 * group + 4, S:2 * S], ACT.Copy).then_inc(cross_copied, 1)

        def split_x(j, norm):
            for t in range(j * BT, (j + 1) * BT):
                ins = act_f(xs[:, t, 0, :], x_res[:, t, :], ACT.Copy, scale=param("gain", norm * KT + t))
            ins.then_inc(xs_hi, 1)
            if j or norm:
                eng.wait_ge(ss_added, 4 * norm + j)
            act_f(buf_g[:, :, :], x_res[:, j * BT:(j + 1) * BT, :], ACT.Square).then_inc(squared, 1)

        def residual(stage, j, n, used, group, norm):
            if stage == 2:
                copy_cross(n, used, group)
            if stage == 3 and norm is not None:
                eng.wait_ge(acc_drained, n + 1)
                split_x(j, norm)

        def stats(norm):
            eng.wait_ge(stat_read, norm + 1)
            act_f(stat_y, stat_v, ACT.Abs_reciprocal_sqrt).then_inc(stat_rsq, 1)

        def mlp_post(stage, ph, half, j):
            n, k = ph.n_up + 2 * j + half, ph.layer * 2 * PAIRS + 2 * j + half
            buf = buf_v if half else buf_g
            if stage == 2:
                copy_cross(n, chunk_end(ph.q_up + 4 * j + 2 * half, KC - 1), half)
            if stage == 3:
                eng.wait_ge(normed, ph.normed_up + 2 * j + half + 1)
                for t in range(BT):
                    w = conv_at(ph.layer, FFN_TAPS - 1, half, j, t)
                    b = conv_b_at(ph.layer, half, j, t)
                    ins = act_f(buf[:, t, :], h[:, t, :], ACT.Identity, scale=w, bias=b)
                ins.then_inc(tap_first, 1)
            if stage == 6 and half == 0:
                eng.wait_ge(conv_done, k + 1)
                act_f(buf_g[:, :, :], buf_g[:, :, :], ACT.Gelu_apprx_tanh).then_inc(gelu_done, 1)
            if stage == 7 and half == 1:
                g = ph.layer * PAIRS + j
                eng.wait_ge(prod_ready, g + 1)
                act_f(act[:, bass.ds(j * BT, BT), 0, :], buf_v[:, :, :], ACT.Copy).then_inc(act_hi, 1)

        def conv_at(layer, tap, half, j, t):
            base = PARAM_AT["ffn_conv_w"] + (layer * FFN_TAPS + tap) * 2 * FT + half * FT + t
            return par[:, bass.ds(base + j * BT, 1)]

        def conv_b_at(layer, half, j, t):
            base = PARAM_AT["ffn_conv_b"] + layer * 2 * FT + half * FT + t
            return par[:, bass.ds(base + j * BT, 1)]

        def lru_conv_first(half):
            eng.wait_ge(normed, half + 1)
            for t in range(BT):
                k = half * BT + t
                ins = act_f(xc[:, k, :], h[:, t, :], ACT.Identity, scale=param("lru_conv_w", (LRU_TAPS - 1) * 8 + k),
                            bias=param("lru_conv_b", k))
            ins.then_inc(xc_first, 1)

        def lru_gates(stage, half):
            if stage == 4:
                eng.wait_ge(gates_done, half + 1)
                for t in range(BT):
                    step(act_f(buf_g[:, t, :], tiles(4)[:, t, :], ACT.Sigmoid, bias=param("lru_b_a", half * BT + t)))
            if stage == 5:
                for t in range(BT):
                    ins = act_f(buf_v[:, t, :], tiles(6)[:, t, :], ACT.Sigmoid, bias=param("lru_b_i", half * BT + t))
                ins.then_inc(gates_read, 1)
            if stage == 6:
                step.sync()
                eng.wait_ge(lru_c_ready, 1)
                for t in range(BT):
                    c = half * BT + t
                    ins = act_f(lru_t[:, t, :], buf_g[:, t, :], ACT.Tanh, scale=lru_c[:, c:c + 1])
                ins.then_inc(lru_tanh, 1)

        def lru_root(half):
            eng.wait_ge(lru_tanh, half + 1)
            act_f(buf_g[:, :, :], lru_t[:, :, :], ACT.Sqrt, scale=-1.0).then_inc(lru_sqrt, 1)

        def mix_split(k, first_tile, src):
            eng.wait_ge(mix_prod, k + 1)
            if k == 0:
                eng.wait_ge(line_stored, 16)
            act_f(act[:, first_tile:first_tile + BT, 0, :], src, ACT.Copy).then_inc(mix_hi, 1)

        def gelu_branch(half):
            eng.wait_ge(normed, 3 + half)
            act_f(gl_gelu[:, half * BT:(half + 1) * BT, :], h[:, :, :], ACT.Gelu_apprx_tanh).then_inc(gelu_gl, 1)

        def silu_gate(grp):
            eng.wait_ge(normed, (7, 10)[grp])
            act_f(ret_gate[:, :, :], h[:, :, :], ACT.Silu).then_inc(gate_silu, 1)

        def ret_square(grp):
            eng.wait_ge(ret_out, grp + 1)
            act_f(ret_sq[:, :, :], tiles(6), ACT.Square).then_inc(ret_squared, 1)

        def ret_rsqrt(grp):
            eng.wait_ge(ret_stat_read, grp + 1)
            act_f(buf_g[:, 0:2, :], buf_g[:, 2:4, :], ACT.Abs_reciprocal_sqrt).then_inc(ret_rsq, 1)

        def qk_square(i, is_k):
            src = ak if is_k else aq
            eng.wait_ge(normed, phases[1].normed_in + 2 * i + is_k + 1)
            act_f(att_sq[:, :, :], src[:, i % 2, :, :], ACT.Square).then_inc(qk_squared, 1)

        def qk_rsqrt(i, is_k):
            eng.wait_ge(qk_stat_read, 2 * i + is_k + 1)
            act_f(buf_g[:, :, :], buf_v[:, :, :], ACT.Abs_reciprocal_sqrt).then_inc(qk_rsq, 1)

        def exps(i):
            eng.wait_ge(negmax_ready, i + 1)
            for b in range(BT):
                for r, part in enumerate((slice(0, P), slice(P, 3 * P))):
                    k = 2 * b + r
                    ins = act_f(probs[:, b, part], probs[:, b, part], ACT.Exp, bias=small[:, 1, k:k + 1],
                                accum_out=small[:, 2, k:k + 1])
            ins.then_inc(exp_done, 1)

        def copy_turned(i):
            eng.wait_ge(turned, i + 1)
            act_f(probs_t[:, :, :], ps[:, 4:8, 0:3 * P], ACT.Copy).then_inc(turned_copied, 1)

        def att_split(i):
            eng.wait_ge(pv_done, i + 1)
            act_f(act[:, i * BT:(i + 1) * BT, 0, :], tiles(4), ACT.Copy).then_inc(mix_hi, 1)

        def even_post(b, stage):
            ph = phases[0]
            if stage == 2 and b and EVEN_BLOCKS[b - 1][0] != "v":
                copy_cross(b - 1, RING * (ph.q_in + 2 * b), EVEN_GROUPS[b - 1])
            if b in (1, 2) and stage == 3:
                lru_conv_first(b - 1)
            if b in (2, 5):
                lru_gates(stage, (2, 5).index(b))
            if b in (3, 6) and stage == 4:
                lru_root((3, 6).index(b))
            if b in (4, 7) and stage == 6:
                half = (4, 7).index(b)
                mix_split(half, 8 + half * BT, buf_v[:, :, :])
            if b in (3, 4) and stage == 3:
                gelu_branch(b - 3)
            if b in (8, 12) and stage == 3:
                silu_gate((8, 12).index(b))
            if (b, stage) in ((8, 4), (12, 1)):
                ret_square((8, 12).index(b))
            if (b, stage) in ((8, 7), (12, 4)):
                ret_rsqrt((8, 12).index(b))
            if (b, stage) in ((9, 2), (12, 5)):
                grp = (9, 12).index(b)
                mix_split(2 + grp, grp * BT, ret_o[:, :, :])

        def odd_post(b, stage):
            ph = phases[1]
            if stage == 2 and b and ODD_BLOCKS[b - 1][0] != "v":
                copy_cross(ph.n_in + b - 1, RING * (ph.q_in + 2 * b), ODD_GROUPS[b - 1])
            i, kind = b // 3, b % 3
            if b in (4, 7, 10) and stage == 3:
                copy_turned(i - 1)
            if kind in (1, 2):
                if stage == 3:
                    qk_square(i, kind - 1)
                if stage == 5:
                    qk_rsqrt(i, kind - 1)
            if (b, stage) in ((3, 5), (6, 5), (9, 5), (12, 2)):
                exps(i - 1)
            if (b, stage) == (12, 3):
                copy_turned(3)
            if (b, stage) in ((4, 7), (7, 7), (11, 4), (12, 4)):
                att_split((4, 7, 11, 12).index(b))

        eng.wait_ge(const_loaded, 16)

        for ph in phases:
            l = ph.layer
            post = odd_post if l else even_post
            for b in range(INB):
                for c in range(KC):
                    if (l, b, c % 2) == (0, 0, 0):
                        eng.wait_ge(x_loaded[c // 2], 16)
                        split_x(c // 2, 0)
                    split(ph.q_in + 2 * b, c)
                    if b == 0 and l:
                        residual(c, 3, phases[0].n_down + 3, RING * ph.q_in, 1, 2)
                    if (l, b, c) == (0, 0, 5):
                        eng.wait_ge(line_done, 1)
                        act_f(line[0:HEADS, :], ps[0:HEADS, 5, 0:3 * P], ACT.Copy).then_inc(line_copied, 1)
                    if (l, b, c) == (0, 1, 7):
                        eng.wait_ge(lam_abs, 1)
                        act_f(small[:, 1, :], small[:, 0, :], ACT.Exp, scale=-1.0).then_inc(lam_exp, 1)
                    post(b, c)
                    if b == 0 and c == 7:
                        stats(2 * l)
            for b in range(OUTB):
                for c in range(KC):
                    split(ph.q_out + 2 * b, c)
                    if b == 0:
                        post(INB, c)
                    else:
                        residual(c, b - 1, ph.n_out + b - 1, RING * (ph.q_out + 2 * b), (b - 1) % 2, 2 * l + 1)
            for c in range(KC):
                split(ph.q_up, c)
                residual(c, 3, ph.n_out + 3, RING * ph.q_up, 1, 2 * l + 1)
                if c == 7:
                    stats(2 * l + 1)
            for c in range(KC):
                split(ph.q_up + 2, c)
                mlp_post(c, ph, 0, 0)
            with eng.Fori(1, PAIRS) as j:
                for c in range(KC):
                    split(ph.q_up + 4 * j, c)
                    mlp_post(c, ph, 1, j - 1)
                for c in range(KC):
                    split(ph.q_up + 4 * j + 2, c)
                    mlp_post(c, ph, 0, j)
            for b in range(OUTB):
                for c in range(FC):
                    split(ph.q_down, FC * b + c)
                    if b == 0:
                        mlp_post(c, ph, 1, PAIRS - 1)
                    else:
                        residual(c, b - 1, ph.n_down + b - 1, RING * ph.q_down + FC * b, (b - 1) % 2, None if l else 2)
        copy_cross(phases[1].n_down + 3, RING * 2 * LAYER_TURNS, 1)

    @block.tensor
    def _(pe):
        mm = nc.tensor.matmul

        def chunk_products(q, c, src, kt, group, first, last):
            s, turn = c % RING, q + c // RING
            pe.wait_ge(lo_ready, RING * turn + s + 1)
            for u in range(CT):
                for m in range(BT):
                    bank, cols = 4 * group + m, slice(m * P, (m + 1) * P)
                    rhs = src[:, kt + u, :, :].rearrange("p a s -> p (a s)")
                    mm(ps[:, bank, :], w_hi[:, s, u, cols], rhs, start=first and u == 0, stop=False)
                    ins = mm(ps[:, bank, 0:S], w_lo[:, s, u, cols], rhs[:, 0:S], start=False, stop=last and u == CT - 1)
            ins.then_inc(chunk_used, 1)

        def chunk_values(q, c, group, first, last):
            s, turn = c % RING, q + c // RING
            pe.wait_ge(lo_ready, RING * turn + s + 1)
            for u in range(CT):
                for t in range(2):
                    x_hi, x_lo = (xs[:, CT * (c % KC) + u, a, t * P:(t + 1) * P] for a in range(2))
                    out = ps[:, 4 * group + t, :]
                    mm(out, x_hi, w_hi[:, s, u, :], start=first and u == 0, stop=False)
                    mm(out, x_hi, w_lo[:, s, u, :], start=False, stop=False)
                    ins = mm(out, x_lo, w_hi[:, s, u, :], start=False, stop=last and u == CT - 1)
            ins.then_inc(chunk_used, 1)

        def stats(norm):
            pe.wait_ge(ss_ready, norm + 1)
            mm(ps[:, 4, 0:S], ones[:, :], sumsq[:, :], start=True, stop=True)
            for t in range(2):
                ins = mm(ps[:, 4, S + t:S + t + 1], sumsq[:, t * P:(t + 1) * P], ones[:, 0:1], start=True, stop=True)
            ins.then_inc(stat_summed, 1)

        def lru_gate_products(half):
            pe.wait_ge(xc_ready, half + 1)
            pe.wait_ge(acc_drained, (2, 4)[half])
            for g in range(2):
                for t in range(BT):
                    ins = mm(tiles(4 + 2 * g)[:, t, :], gates_w[:, g, half * BT + t, :], xc[:, half * BT + t, :],
                             start=True, stop=True)
            ins.then_inc(gates_done, 1)

        def ret_scores(grp):
            pe.wait_ge(rot_ready, 2 * grp + 2)
            pe.wait_ge(acc_drained, (7, 10)[grp])
            for a in range(2):
                for keys, queries, to in ((slice(0, P), slice(0, S), slice(0, S)),
                                          (slice(P, S), slice(P, S), slice(S, S + P))):
                    for e in range(2):
                        ins = mm(ps[:, 4 + a, to], rk[:, 2 * a + e, keys], rq[:, 2 * a + e, queries],
                                 start=e == 0, stop=e == 1)
            ins.then_inc(ret_scored, 1)

        def weighted_values(out, values, cols, weights):
            mm(out, values[:, 0, cols], weights[:, 0:S], start=True, stop=False, skip_group_check=True)
            return mm(out[:, P:S], values[:, 1, cols], weights[:, S:S + P], start=False, stop=True, skip_group_check=True)

        def ret_values(grp):
            pe.wait_ge(ret_s_ready, grp + 1)
            pe.wait_ge(acc_drained, (6, 10)[grp] + 1)
            for a in range(2):
                for e in range(2):
                    cols = slice((2 * a + e) * P, (2 * a + e + 1) * P)
                    ins = weighted_values(tiles(6)[:, 2 * a + e, :], rv, cols, ret_s[:, a, :])
            ins.then_inc(ret_out, 1)

        def ret_sums(grp):
            pe.wait_ge(ret_squared, grp + 1)
            for a in range(2):
                for e in range(2):
                    ins = mm(ps[:, 4, a * S:(a + 1) * S], ones[:, :], ret_sq[:, 2 * a + e, :], start=e == 0, stop=e == 1)
            ins.then_inc(ret_summed, 1)

        def even_extra(b, c):
            if (b, c) in ((2, 3), (5, 0)):
                lru_gate_products((2, 5).index(b))
            if (b, c) in ((3, 0), (6, 0)):
                pe.wait_ge(gates_read, b // 3)
            if (b, c) in ((7, 3), (11, 0)):
                ret_scores((7, 11).index(b))
            if (b, c) == (9, 0):
                pe.wait_ge(ret_copied, 1)
                pe.wait_ge(ret_stat_read, 1)
            if b in (8, 12) and c == 0:
                ret_values((8, 12).index(b))
            if (b, c) in ((8, 6), (12, 3)):
                ret_sums((8, 12).index(b))

        def qk_sums(i, is_k):
            pe.wait_ge(qk_squared, 2 * i + is_k + 1)
            if i:
                pe.wait_ge(turned_copied, i)
            flat = att_sq[:, :, :].rearrange("p t s -> p (t s)")
            for u in range(2):
                ins = mm(ps[:, 6 + u, :], ones[:, :], flat[:, u * NB:(u + 1) * NB], start=True, stop=True)
            ins.then_inc(qk_summed, 1)

        def scores(i):
            pe.wait_ge(qk_ready, 2 * i + 2)
            if i < 3:
                pe.wait_ge(acc_drained, phases[1].n_in + 3 * i + 3)
            else:
                pe.wait_ge(mix_lo, 4 + i)
            for b in range(BT):
                q, k = aq[:, i % 2, b, :], ak[:, i % 2, b, :]
                mm(ps[:, 4 + b, 0:P], q[:, 0:P], k[:, 0:P], start=True, stop=True)
                ins = mm(ps[:, 4 + b, P:3 * P], q[:, P:S], k[:, 0:S], start=True, stop=True)
            ins.then_inc(scored, 1)

        def turn(i):
            pe.wait_ge(probs_ready, i + 1)
            for b in range(BT):
                for r in range(3):
                    part = slice(r * P, (r + 1) * P)
                    ins = nc.tensor.transpose(ps[:, 4 + b, part], probs[:, b, part], ident[:, :])
            ins.then_inc(turned, 1)

        def att_values(i):
            pe.wait_ge(turned_copied, i + 1)
            pe.wait_ge(acc_drained, phases[1].n_in + 3 * i + 3)
            for b in range(BT):
                cols = slice(b * P, (b + 1) * P)
                ins = weighted_values(tiles(4)[:, b, :], av[:, i % 2], cols, probs_t[:, b, :])
            ins.then_inc(pv_done, 1)

        def odd_extra(b, c):
            i, kind = b // 3, b % 3
            if kind in (1, 2) and c == 3:
                qk_sums(i, kind - 1)
            if (b, c) in ((3, 3), (6, 3), (9, 3), (12, 0)):
                scores(i - 1)
            if (b, c) in ((4, 0), (7, 0), (10, 0), (12, 3)):
                turn((4, 7, 10, 12).index(b))
            if (b, c) in ((4, 6), (7, 6), (11, 0), (12, 4)):
                att_values((4, 7, 11, 12).index(b))
            if (b, c) in ((5, 0), (8, 0)):
                pe.wait_ge(mix_lo, 4 + i)

        def bias_line_product():
            pe.wait_ge(consts_set, 2)
            pe.wait_ge(work_loaded, 16 * 6)
            mm(ps[0:HEADS, 5, 0:3 * P], rel_ext[0:REL_BUCKETS + 1, :], bucket_t[0:REL_BUCKETS + 1, :],
               start=True, stop=True).then_inc(line_done, 1)

        for ph in phases:
            l = ph.layer
            extra = odd_extra if l else even_extra
            blocks, groups = (ODD_BLOCKS, ODD_GROUPS) if l else (EVEN_BLOCKS, EVEN_GROUPS)
            for b in range(INB):
                for c in range(KC):
                    extra(b, c)
                    if b == 0 and c % 2 == 0:
                        pe.wait_ge(xs_lo, 4 * (2 * l) + c // 2 + 1)
                    if b == 0 and c == 6:
                        pe.wait_ge(xs_lo, 4 * (2 * l) + 4)
                        stats(2 * l)
                    if (l, b, c) == (0, 0, 5):
                        bias_line_product()
                    group = groups[b]
                    if c == 0 and (b or l):
                        same = [k for k in range(b) if groups[k] == group]
                        pe.wait_ge(acc_drained, ph.n_in + (same[-1] + 1 if same else group - 1) if same or l else 1)
                    if b == 1 and c == 0:
                        pe.wait_ge(rstd_ready, 2 * l + 1)
                    if blocks[b][0] == "v":
                        chunk_values(ph.q_in + 2 * b, c, group, c == 0, c == KC - 1)
                    else:
                        chunk_products(ph.q_in + 2 * b, c, xs, CT * c, group, c == 0, c == KC - 1)
            for b in range(OUTB):
                for c in range(KC):
                    if b == 0:
                        extra(INB, c)
                    if c == 0:
                        pe.wait_ge(acc_drained, ph.n_out + b if b == 0 else ph.n_out + b - 1)
                    kt = CT * MIX_ORDER[l][c]
                    if b == 0 and c % 2 == 0:
                        pe.wait_ge(mix_lo, 4 * l + c // 2 + 1)
                    if b == 1 and c == 0:
                        if l == 0:
                            pe.wait_ge(ret_stat_read, 2)
                    chunk_products(ph.q_out + 2 * b, c, act, kt, b % 2, c == 0, c == KC - 1)
            for half in range(2):
                for c in range(KC):
                    if half == 0 and c % 2 == 0:
                        pe.wait_ge(xs_lo, 4 * (2 * l + 1) + c // 2 + 1)
                    if c == 0:
                        pe.wait_ge(acc_drained, ph.n_up + half - 1)
                    if half == 0 and c == 6:
                        pe.wait_ge(acc_drained, ph.n_up)
                        stats(2 * l + 1)
                    if half == 1 and c == 0:
                        pe.wait_ge(rstd_ready, 2 * l + 2)
                    chunk_products(ph.q_up + 2 * half, c, xs, CT * c, half, c == 0, c == KC - 1)
            with pe.Fori(1, PAIRS) as j:
                for half in range(2):
                    pe.wait_ge(acc_drained, ph.n_up + 2 * j + half - 1)
                    for c in range(KC):
                        chunk_products(ph.q_up + 4 * j + 2 * half, c, xs, CT * c, half, c == 0, c == KC - 1)
            for b in range(OUTB):
                pe.wait_ge(acc_drained, ph.n_down + b - 1)
                for c in range(FC):
                    if b == 0 and c % 2 == 0:
                        pe.wait_ge(act_lo, PAIRS * l + c // 2 + 1)
                    chunk_products(ph.q_down, FC * b + c, act, CT * c, b % 2, c == 0, c == FC - 1)

    @block.vector
    def _(eng):
        v = nc.vector
        stt, tt, ts = v.scalar_tensor_tensor, v.tensor_tensor, v.tensor_scalar
        step = Steps(eng, dve_step)

        def split(q, c):
            s, turn = c % RING, q + c // RING
            eng.wait_ge(hi_ready, RING * turn + s + 1)
            tt(w_lo[:, s, :, :], raw[:, s, :, :], w_hi[:, s, :, :].bitcast(F32), ALU.subtract).then_inc(lo_ready, 1)

        def drain_normed(n, n_cross, n_normed, group, dst):
            eng.wait_ge(cross_copied, n_cross)
            step.sync()
            tt(dst, ps[:, 4 * group:4 * group + 4, 0:S], cross[:, :, :], ALU.add).then_inc(acc_drained, 1)
            eng.wait_ge(acc_drained, n + 1)
            tt(dst, dst, spread(rstd[:, 0:S], BT), ALU.mult).then_inc(normed, 1)
            eng.wait_ge(normed, n_normed)

        def drain_values(n, used, group, dst):
            eng.wait_ge(chunk_used, used)
            step.sync()
            step(ts(dst[:, 0, :], ps[:, 4 * group, :], rstd[:, S:S + 1], None, ALU.mult))
            ts(dst[:, 1, :], ps[:, 4 * group + 1, :], rstd[:, S + 1:S + 2], None, ALU.mult).then_inc(acc_drained, 1)
            eng.wait_ge(acc_drained, n + 1)

        def add_residual(j, n, n_cross, group):
            eng.wait_ge(cross_copied, n_cross)
            x = x_res[:, j * BT:(j + 1) * BT, :]
            step.sync()
            step(tt(x, x, cross[:, :, :], ALU.add))
            step.sync()
            tt(x, x, ps[:, 4 * group:4 * group + 4, 0:S], ALU.add).then_inc(acc_drained, 1)
            eng.wait_ge(acc_drained, n + 1)

        def split_x(j, norm):
            eng.wait_ge(xs_hi, 4 * norm + j + 1)
            for t in range(j * BT, (j + 1) * BT):
                ins = stt(out=xs[:, t, 1, :], in0=x_res[:, t, :], scalar=param("gain", norm * KT + t),
                          in1=xs[:, t, 0, :].bitcast(F32), op0=ALU.mult, op1=ALU.subtract)
            ins.then_inc(xs_lo, 1)

        def sum_squares(j, norm):
            eng.wait_ge(squared, 4 * norm + j + 1)
            if j == 0 and norm:
                eng.wait_ge(rstd_ready, norm)
            step.sync()
            dst = sumsq[:, :] if j == 0 else stat_sum
            v.tensor_reduce(dst, buf_g[:, :, :].rearrange("p t s -> p s t"), AX.X, ALU.add).then_inc(ss_added, 1)
            eng.wait_ge(ss_added, 4 * norm + j + 1)
            if j:
                ins = tt(sumsq[:, :], sumsq[:, :], stat_sum, ALU.add)
                if j == 3:
                    ins.then_inc(ss_ready, 1)
                    eng.wait_ge(ss_ready, norm + 1)
                else:
                    step(ins)

        def residual(stage, j, n, n_cross, group, norm):
            if stage == 2:
                add_residual(j, n, n_cross, group)
            if stage == 4 and norm is not None:
                split_x(j, norm)
            if stage == 5 and norm is not None:
                sum_squares(j, norm)

        def newton(y, x, t):
            step.sync()
            step(stt(out=t, in0=y, scalar=-0.5, in1=y, op0=ALU.mult, op1=ALU.mult))
            step.sync()
            step(tt(t, t, x, ALU.mult))
            step.sync()

        def stats(norm):
            eng.wait_ge(stat_summed, norm + 1)
            step.sync()
            ts(stat_v, ps[:, 4, 0:S + 2], 1.0 / D, EPS, ALU.mult, ALU.add).then_inc(stat_read, 1)
            eng.wait_ge(stat_read, norm + 1)
            eng.wait_ge(stat_rsq, norm + 1)
            newton(stat_y, stat_v, rstd[:, :])
            stt(out=rstd[:, :], in0=rstd[:, :], scalar=1.5, in1=stat_y, op0=ALU.add, op1=ALU.mult).then_inc(rstd_ready, 1)
            eng.wait_ge(rstd_ready, norm + 1)

        def mlp_post(stage, ph, half, j):
            n, k = ph.n_up + 2 * j + half, ph.layer * 2 * PAIRS + 2 * j + half
            buf = buf_v if half else buf_g
            if stage == 2:
                drain_normed(n, ph.cross_up + 2 * j + half + 1, ph.normed_up + 2 * j + half + 1, half, h[:, :, :])
            if stage == 4:
                eng.wait_ge(tap_first, k + 1)
                for t in range(BT):
                    step(stt(out=buf[:, t, 1:S], in0=h[:, t, 0:S - 1], scalar=conv_at(ph.layer, 1, half, j, t),
                             in1=buf[:, t, 1:S], op0=ALU.mult, op1=ALU.add))
            if stage == 5:
                step.sync()
                for t in range(BT):
                    ins = stt(out=buf[:, t, 2:S], in0=h[:, t, 0:S - 2], scalar=conv_at(ph.layer, 0, half, j, t),
                              in1=buf[:, t, 2:S], op0=ALU.mult, op1=ALU.add)
                    if t < BT - 1:
                        step(ins)
                ins.then_inc(conv_done, 1)
                eng.wait_ge(conv_done, k + 1)
            if half and stage >= 6:
                g = ph.layer * PAIRS + j
                if stage == 6:
                    eng.wait_ge(gelu_done, g + 1)
                    tt(buf_v[:, :, :], buf_v[:, :, :], buf_g[:, :, :], ALU.mult).then_inc(prod_ready, 1)
                    eng.wait_ge(prod_ready, g + 1)
                if stage == 7:
                    eng.wait_ge(act_hi, g + 1)
                    tiles_j = bass.ds(j * BT, BT)
                    tt(act[:, tiles_j, 1, :], buf_v[:, :, :], act[:, tiles_j, 0, :].bitcast(F32),
                       ALU.subtract).then_inc(act_lo, 1)
                    eng.wait_ge(act_lo, g + 1)

        def conv_at(layer, tap, half, j, t):
            base = PARAM_AT["ffn_conv_w"] + (layer * FFN_TAPS + tap) * 2 * FT + half * FT + t
            return par[:, bass.ds(base + j * BT, 1)]

        def lru_constant():
            lam = par[:, PARAM_AT["lru_lambda"]:PARAM_AT["lru_lambda"] + 8]
            a, y, s, z = (small[:, k, :] for k in range(4))
            step(ts(z, lam, -1.0, None, ALU.mult))
            step.sync()
            tt(a, lam, z, ALU.max).then_inc(lam_abs, 1)
            eng.wait_ge(lam_exp, 1)
            step(ts(s, y, 2.0, None, ALU.add))
            step.sync()
            step(v.reciprocal(a, s))
            step.sync()
            step(tt(s, a, y, ALU.mult))
            step.sync()
            step(tt(y, s, s, ALU.mult))
            step.sync()
            step(ts(a, y, 2.0 / (2 * LOG1P_TERMS - 1), 2.0 / (2 * LOG1P_TERMS - 3), ALU.mult, ALU.add))
            for k in range(LOG1P_TERMS - 3, -1, -1):
                step.sync()
                step(tt(a, a, y, ALU.mult))
                step.sync()
                step(ts(a, a, 2.0 / (2 * k + 1), None, ALU.add))
            step.sync()
            step(tt(a, a, s, ALU.mult))
            step(ts(z, z, 0.0, None, ALU.max))
            step.sync()
            step(tt(a, a, z, ALU.add))
            step.sync()
            ts(lru_c[:, :], a, -4.0, None, ALU.mult).then_inc(lru_c_ready, 1)

        def lru_conv(stage, half):
            if stage == 4:
                eng.wait_ge(xc_first, half + 1)
            tap = {4: 2, 5: 1, 6: 0}[stage]
            back = LRU_TAPS - 1 - tap
            step.sync()
            for t in range(BT):
                k = half * BT + t
                ins = stt(out=xc[:, k, back:S], in0=h[:, t, 0:S - back], scalar=param("lru_conv_w", tap * 8 + k),
                          in1=xc[:, k, back:S], op0=ALU.mult, op1=ALU.add)
                if t < BT - 1 or tap:
                    step(ins)
            if tap == 0:
                ins.then_inc(xc_ready, 1)
                eng.wait_ge(xc_ready, half + 1)

        def lru_decay(stage, half):
            if stage == 4:
                eng.wait_ge(lru_tanh, half + 1)
                step.sync()
                step(ts(lru_w[:, :, :], lru_t[:, :, :], -1.0, 1.0, ALU.mult, ALU.add))
            if stage in (5, 6):
                step.sync()
                part = slice(2 * (stage - 5), 2 * (stage - 5) + 2)
                step(v.reciprocal(lru_w[:, part, :], lru_w[:, part, :]))
            if stage == 7:
                eng.wait_ge(lru_sqrt, half + 1)
                step.sync()
                step(stt(out=lru_t[:, :, :], in0=lru_t[:, :, :], scalar=1.0, in1=lru_w[:, :, :], op0=ALU.add, op1=ALU.mult))

        def lru_scan(stage, half):
            if stage == 3:
                step.sync()
                step(stt(out=buf_g[:, :, :], in0=buf_g[:, :, :], scalar=2.0, in1=lru_w[:, :, :], op0=ALU.mult, op1=ALU.mult))
                eng.wait_ge(gates_read, half + 1)
                step.sync()
                step(tt(buf_g[:, :, :], buf_g[:, :, :], buf_v[:, :, :], ALU.mult))
            if stage == 4:
                step.sync()
                step(tt(buf_g[:, :, :], buf_g[:, :, :], xc[:, half * BT:(half + 1) * BT, :], ALU.mult))
            if stage == 5:
                step.sync()
                for t in range(BT):
                    step(v.tensor_tensor_scan(buf_v[:, t, :], lru_t[:, t, :], buf_g[:, t, :], 0.0, ALU.mult, ALU.add))
            if stage == 6:
                eng.wait_ge(gelu_gl, half + 1)
                step.sync()
                tt(buf_v[:, :, :], buf_v[:, :, :], gl_gelu[:, half * BT:(half + 1) * BT, :], ALU.mult).then_inc(mix_prod, 1)
            if stage == 7:
                mix_split(half, 8 + half * BT, buf_v[:, :, :])

        def mix_split(k, first_tile, src):
            eng.wait_ge(mix_hi, k + 1)
            part = act[:, first_tile:first_tile + BT, :, :]
            tt(part[:, :, 1, :], src, part[:, :, 0, :].bitcast(F32), ALU.subtract).then_inc(mix_lo, 1)
            eng.wait_ge(mix_lo, k + 1)

        def rotate(stage, k, dst):
            if stage == 5:
                if k == 0:
                    eng.wait_ge(work_loaded, 16 * 6)
                step(tt(rot_a[:, :, :], h[:, :, :], spread(rope_t[:, 0, :], BT), ALU.mult))
                step(tt(rot_b[:, :, :], h[:, :, :], spread(rope_t[:, 1, :], BT), ALU.mult))
            if stage == 7:
                a, b, d = (m[:, :, :].rearrange("p (h u) s -> p h u s", u=2) for m in (rot_a, rot_b, dst))
                step.sync()
                step(tt(d[:, :, 0, :], a[:, :, 0, :], b[:, :, 1, :], ALU.subtract))
                tt(d[:, :, 1, :], b[:, :, 0, :], a[:, :, 1, :], ALU.add).then_inc(rot_ready, 1)
                eng.wait_ge(rot_ready, k + 1)

        def ret_decay(grp):
            eng.wait_ge(ret_scored, grp + 1)
            step.sync()
            for a in range(2):
                d = decay_t[:, 2 * grp + a, :]
                step(tt(ret_s[:, a, 0:S], ps[:, 4 + a, 0:S], d, ALU.mult))
                ins = tt(ret_s[:, a, S:S + P], ps[:, 4 + a, S:S + P], d[:, 0:P], ALU.mult)
                if a == 0:
                    step(ins)
            ins.then_inc(ret_s_ready, 1)

        def ret_copy(grp):
            eng.wait_ge(ret_squared, grp + 1)
            step.sync()
            v.tensor_copy(ret_o[:, :, :], tiles(6)).then_inc(ret_copied, 1)

        def ret_norm(stage, grp):
            y, x, t = buf_g[:, 0:2, :], buf_g[:, 2:4, :], buf_v[:, 0:2, :]
            if stage == 0:
                eng.wait_ge(ret_summed, grp + 1)
                eng.wait_ge(ret_copied, grp + 1)
                step.sync()
                ts(x, tiles(4, 2), 1.0 / RET_DIM, EPS, ALU.mult, ALU.add).then_inc(ret_stat_read, 1)
                eng.wait_ge(ret_stat_read, grp + 1)
            elif stage == 1:
                eng.wait_ge(ret_rsq, grp + 1)
                newton(y, x, t)
                step(stt(out=y, in0=t, scalar=1.5, in1=y, op0=ALU.add, op1=ALU.mult))
            elif stage == 2:
                step.sync()
                for k in range(BT):
                    step(stt(out=ret_o[:, k, :], in0=ret_o[:, k, :], scalar=param("ret_norm", grp * BT + k),
                             in1=y[:, k // 2, :], op0=ALU.mult, op1=ALU.mult))
                eng.wait_ge(gate_silu, grp + 1)
                step.sync()
                tt(ret_o[:, :, :], ret_o[:, :, :], ret_gate[:, :, :], ALU.mult).then_inc(mix_prod, 1)
            else:
                mix_split(2 + grp, grp * BT, ret_o[:, :, :])

        def even_post(b, stage):
            ph = phases[0]
            if stage == 2 and b:
                kind = EVEN_BLOCKS[b - 1][0]
                if kind == "v":
                    drain_values(b - 1, RING * (ph.q_in + 2 * b), EVEN_GROUPS[b - 1], rv)
                else:
                    values_before = sum(x[0] == "v" for x in EVEN_BLOCKS[:b])
                    h_free(b)
                    drain_normed(b - 1, b - values_before, b - values_before, EVEN_GROUPS[b - 1], h[:, :, :])
            if b in (1, 2) and stage in (4, 5, 6):
                lru_conv(stage, b - 1)
            if b in (3, 6):
                lru_decay(stage, (3, 6).index(b)) if stage >= 4 else None
            if b in (4, 7):
                lru_scan(stage, (4, 7).index(b))
            if b in (5, 6, 9, 10) and stage in (5, 7):
                k = (5, 6, 9, 10).index(b)
                rotate(stage, k, rk if k % 2 else rq)
            if (b, stage) in ((7, 7), (11, 5)):
                ret_decay((7, 11).index(b))
            if (b, stage) in ((8, 4), (12, 1)):
                ret_copy((8, 12).index(b))
            if (b, stage) in ((8, 7), (12, 4)):
                ret_norm(0, (8, 12).index(b))
            if (b, stage) in ((9, 0), (12, 4)):
                ret_norm(1, (9, 12).index(b))
            if (b, stage) in ((9, 1), (12, 4)):
                ret_norm(2, (9, 12).index(b))
            if (b, stage) in ((9, 3), (12, 5)):
                ret_norm(3, (9, 12).index(b))

        def h_free(b):
            last = EVEN_BLOCKS[b - 2][0] if b >= 2 else None
            if b == 1:
                return
            if last == "xl":
                eng.wait_ge(xc_first, (2, 3).index(b) + 1)
            if last == "gl":
                eng.wait_ge(gelu_gl, (4, 5).index(b) + 1)
            if last == "g":
                eng.wait_ge(gate_silu, 1)

        def qk_norm(part, i, is_k):
            k = 2 * i + is_k
            y, x, t = buf_g[:, :, :], buf_v[:, :, :], att_sq[:, :, :]
            dst = (ak if is_k else aq)[:, i % 2, :, :]
            if part == 0:
                eng.wait_ge(qk_summed, k + 1)
                step.sync()
                ts(x, tiles(6), 1.0 / HEAD_DIM if is_k else 1.0, EPS if is_k else EPS * HEAD_DIM,
                   ALU.mult, ALU.add).then_inc(qk_stat_read, 1)
                eng.wait_ge(qk_stat_read, k + 1)
            if part == 1:
                eng.wait_ge(qk_rsq, k + 1)
                newton(y, x, t)
            if part == 2:
                step.sync()
                step(stt(out=y, in0=t, scalar=1.5, in1=y, op0=ALU.add, op1=ALU.mult))
                step.sync()
                stt(out=dst, in0=dst, scalar=param("k_norm" if is_k else "q_norm"), in1=y,
                    op0=ALU.mult, op1=ALU.mult).then_inc(qk_ready, 1)
                eng.wait_ge(qk_ready, k + 1)

        def logits(i):
            eng.wait_ge(scored, i + 1)
            if i == 0:
                eng.wait_ge(bias_loaded, 16)
            step.sync()
            for b in range(BT):
                for r, (part, n_keys) in enumerate(((slice(0, P), P), (slice(P, 3 * P), S))):
                    g = bias[:, i * BT + b, :]
                    tab = bass.AP(g.tensor, g.offset + n_keys - 1, [g.ap[0], [-1, n_keys]])
                    k = 2 * b + r
                    step(v.tensor_tensor_reduce(out=probs[:, b, part], in0=ps[:, 4 + b, part], in1=tab, scale=1.0,
                                                scalar=-3e38, op0=ALU.add, op1=ALU.max, accum_out=small[:, 0, k:k + 1]))
            step.sync()
            ts(small[:, 1, :], small[:, 0, :], -1.0, None, ALU.mult).then_inc(negmax_ready, 1)

        def normalise(i):
            eng.wait_ge(exp_done, i + 1)
            step(v.reciprocal(small[:, 3, :], small[:, 2, :]))
            step.sync()
            for b in range(BT):
                for r, part in enumerate((slice(0, P), slice(P, 3 * P))):
                    k = 2 * b + r
                    ins = ts(probs[:, b, part], probs[:, b, part], small[:, 3, k:k + 1], None, ALU.mult)
                    if k < 2 * BT - 1:
                        step(ins)
            ins.then_inc(probs_ready, 1)
            eng.wait_ge(probs_ready, i + 1)

        def odd_post(b, stage):
            ph = phases[1]
            if stage == 2 and b:
                kind, i, _ = ODD_BLOCKS[b - 1]
                if kind == "v":
                    drain_values(ph.n_in + b - 1, RING * (ph.q_in + 2 * b), ODD_GROUPS[b - 1], av[:, i % 2])
                else:
                    k = 2 * i + (kind == "k") + 1
                    drain_normed(ph.n_in + b - 1, ph.cross_in + k, ph.normed_in + k, ODD_GROUPS[b - 1],
                                 (ak if kind == "k" else aq)[:, i % 2, :, :])
            i, kind = b // 3, b % 3
            if kind in (1, 2) and stage in (4, 6, 7):
                qk_norm((4, 6, 7).index(stage), i, kind - 1)
            if (b, stage) in ((3, 4), (6, 4), (9, 4), (12, 2)):
                logits(i - 1)
            if (b, stage) in ((3, 6), (6, 6), (9, 6), (12, 3)):
                normalise(i - 1)
            if (b, stage) in ((4, 7), (7, 7), (11, 7), (12, 5)):
                k = (4, 7, 11, 12).index(b)
                eng.wait_ge(mix_hi, 4 + k + 1)
                part = act[:, k * BT:(k + 1) * BT, :, :]
                tt(part[:, :, 1, :], tiles(4), part[:, :, 0, :].bitcast(F32), ALU.subtract).then_inc(mix_lo, 1)

        eng.wait_ge(const_loaded, 16)

        for ph in phases:
            l = ph.layer
            post = odd_post if l else even_post
            for b in range(INB):
                for c in range(KC):
                    if (l, b, c % 2) == (0, 0, 0):
                        split_x(c // 2, 0)
                    split(ph.q_in + 2 * b, c)
                    if (l, b, c % 2) == (0, 0, 0):
                        sum_squares(c // 2, 0)
                    if (l, b, c) == (0, 1, 7):
                        lru_constant()
                    if b == 0 and l:
                        residual(c, 3, phases[0].n_down + 3, ph.cross_in, 1, 2)
                    post(b, c)
                    if b == 0 and c == 7:
                        stats(2 * l)
            for b in range(OUTB):
                for c in range(KC):
                    split(ph.q_out + 2 * b, c)
                    if b == 0:
                        post(INB, c)
                    else:
                        residual(c, b - 1, ph.n_out + b - 1, ph.cross_out + b, (b - 1) % 2, 2 * l + 1)
            for c in range(KC):
                split(ph.q_up, c)
                residual(c, 3, ph.n_out + 3, ph.cross_up, 1, 2 * l + 1)
                if c == 7:
                    stats(2 * l + 1)
            for c in range(KC):
                split(ph.q_up + 2, c)
                mlp_post(c, ph, 0, 0)
            entered, per_pair = step.n, 2 * (2 * BT - 1)
            with eng.Fori(1, PAIRS) as j:
                step.base = (j - 1) * per_pair
                for c in range(KC):
                    split(ph.q_up + 4 * j, c)
                    mlp_post(c, ph, 1, j - 1)
                for c in range(KC):
                    split(ph.q_up + 4 * j + 2, c)
                    mlp_post(c, ph, 0, j)
                assert step.n == entered + per_pair
            step.base, step.n = 0, entered + (PAIRS - 1) * per_pair
            for b in range(OUTB):
                for c in range(FC):
                    split(ph.q_down, FC * b + c)
                    if b == 0:
                        mlp_post(c, ph, 1, PAIRS - 1)
                    else:
                        residual(c, b - 1, ph.n_down + b - 1, ph.cross_down + b, (b - 1) % 2, None if l else 2)
        add_residual(3, phases[1].n_down + 3, phases[1].cross_down + OUTB, 1)

    block.__exit__(None, None, None)


def tables():
    half = RET_DIM // 2
    freqs = np.float32(10000.0) ** (-np.arange(half, dtype=np.float32) / np.float32(half))
    ang = freqs[:, None] * np.arange(S, dtype=np.float32)[None, :]
    rope = np.stack([np.cos(ang), np.sin(ang)], axis=1).astype(np.float32)
    log_g = np.log1p(-np.exp2(-5.0 - np.arange(RET_HEADS)))
    dist = np.arange(S)[None, :] - np.arange(P)[:, None]
    decay = np.where(dist >= 0, np.exp(log_g[:, None, None] * np.maximum(dist, 0)), 0.0) * RET_DIM ** -0.5
    m = np.arange(3 * P) - (P - 1)
    exact = REL_BUCKETS // 2
    far = np.maximum(m, 1).astype(np.float32) / np.float32(exact)
    large = exact + (np.log(far) / np.float32(np.log(REL_MAX_DIST / exact)) * (REL_BUCKETS - exact)).astype(np.int32)
    bucket = np.where(m < exact, m, np.minimum(large, REL_BUCKETS - 1))
    bucket = np.where(m < 0, REL_BUCKETS, bucket)
    buckets = (np.arange(REL_BUCKETS + 1)[:, None] == bucket[None, :]).astype(np.float32)
    return rope, decay.transpose(1, 0, 2).astype(np.float32), buckets, np.eye(P, dtype=np.float32)


def kernel(**inputs):
    import concourse.bacc as bacc
    from concourse.bass_utils import run_bass_kernel_spmd

    a = {k: np.asarray(v) for k, v in inputs.items()}

    def by_tile(v):
        return v.reshape(-1, P).T

    gain = np.concatenate([a["norm_mix"][0], a["norm_ffn"][0], a["norm_mix"][1], a["norm_ffn"][1]])
    fields = dict(gain=gain, **{k: a[k] for k, _ in PARAM_FIELDS if k != "gain"})
    rope, decay, buckets, identity = tables()
    arrays = {
        "x_t": a["x"][0].T.reshape(KT, P, S).transpose(1, 0, 2),
        "params": np.concatenate([by_tile(fields[k]) for k, _ in PARAM_FIELDS], axis=1),
        "w_gates": np.stack([a["lru_w_a"][0], a["lru_w_i"][0]]).transpose(2, 0, 1, 3),
        "rope": rope, "decay": decay, "rel_bias": a["rel_bias"], "buckets": buckets, "identity": identity,
        "w_in0": a["ev_w_in"][0], "w_out0": a["ev_w_out"][0],
        "w_up0": a["ffn_w_up"][0], "w_down0": a["ffn_w_down"][0],
        "w_in1": a["od_w_in"][0], "w_out1": a["od_w_out"][0],
        "w_up1": a["ffn_w_up"][1], "w_down1": a["ffn_w_down"][1],
    }
    arrays = {k: np.ascontiguousarray(v) for k, v in arrays.items()}
    nc = bacc.Bacc("TRN2", target_bir_lowering=False, num_devices=1)
    aps = [nc.dram_tensor(k, v.shape, mybir.dt.from_np(v.dtype), kind="ExternalInput").ap() for k, v in arrays.items()]
    out = nc.dram_tensor("out_t", (P, KT, S), F32, kind="ExternalOutput").ap()
    build(nc, *aps, out)
    r = run_bass_kernel_spmd(nc, [arrays], core_ids=[0])
    y = r.results[0]["out_t"]
    return np.ascontiguousarray(y.transpose(1, 0, 2).reshape(D, S).T)[None]
```
